# Optimizing a Trainium2 kernel written in Bass

```python
import jax
import jax.numpy as jnp
from jax import lax
import numpy as np

D_MODEL = 2048
BATCH = 1
SEQ = 512
DEPTH = 1

CHUNK = 64
ATT_HEADS = 16
ATT_KV_HEADS = 4
ATT_GROUP = ATT_HEADS // ATT_KV_HEADS
ATT_HEAD_DIM = 64
ATT_Q_WIDTH = ATT_HEADS * ATT_HEAD_DIM
ATT_KV_WIDTH = ATT_KV_HEADS * ATT_HEAD_DIM
WINDOW = 128
WINDOW_CHUNKS = WINDOW // CHUNK
HG_HEADS = 8
HG_KEY_DIM = 128
HG_VAL_DIM = 128
HG_K_WIDTH = HG_HEADS * HG_KEY_DIM
HG_V_WIDTH = HG_HEADS * HG_VAL_DIM
D_FF = 5504
CONV_WIDTH = 3
N_MOD = 6
EPS = 1e-6
IN_SPLIT_SIZES = (ATT_Q_WIDTH, ATT_KV_WIDTH, ATT_KV_WIDTH, HG_K_WIDTH, HG_K_WIDTH, HG_V_WIDTH, HG_V_WIDTH, D_MODEL, D_MODEL)
IN_WIDTH = ATT_Q_WIDTH + 2 * ATT_KV_WIDTH + 2 * HG_K_WIDTH + 2 * HG_V_WIDTH + 2 * D_MODEL

kernel_name = 'hybrid_swa_sink_hgrn2_convffn_block'

def rms_norm(x, w):
    xf = x.astype(jnp.float32)
    y = xf * lax.rsqrt(jnp.mean(xf * xf, axis=-1, keepdims=True) + EPS)
    return (y * w.astype(jnp.float32)).astype(x.dtype)

def alibi_slopes(n_heads):
    return jnp.exp2(-8.0 * jnp.arange(1, n_heads + 1, dtype=jnp.float32) / n_heads)

def sliding_window_sink_attention(q, k, v, sinks):
    bsz, seq = q.shape[0], q.shape[1]
    n_chunks = seq // CHUNK
    band = WINDOW_CHUNKS * CHUNK
    qc = q.reshape(bsz, n_chunks, CHUNK, ATT_KV_HEADS, ATT_GROUP, ATT_HEAD_DIM)
    kc = k.reshape(bsz, n_chunks, CHUNK, ATT_KV_HEADS, ATT_HEAD_DIM)
    vc = v.reshape(bsz, n_chunks, CHUNK, ATT_KV_HEADS, ATT_HEAD_DIM)

    def banded(t):
        parts = [jnp.pad(t, ((0, 0), (w, 0), (0, 0), (0, 0), (0, 0)))[:, :n_chunks]
                 for w in range(WINDOW_CHUNKS - 1, -1, -1)]
        return jnp.concatenate(parts, axis=2)

    kb, vb = banded(kc), banded(vc)
    s = jnp.einsum('bcqhgd,bckhd->bchgqk', qc, kb).astype(jnp.float32) * (ATT_HEAD_DIM ** -0.5)
    q_pos = (WINDOW_CHUNKS - 1) * CHUNK + jnp.arange(CHUNK)
    k_pos = jnp.arange(band)
    dist = jnp.abs(q_pos[:, None] - k_pos[None, :]).astype(jnp.float32)
    slopes = alibi_slopes(ATT_HEADS).reshape(ATT_KV_HEADS, ATT_GROUP)
    s = s - slopes[:, :, None, None] * dist
    key_chunk = jnp.arange(n_chunks)[:, None] - (WINDOW_CHUNKS - 1) + k_pos[None, :] // CHUNK
    valid = key_chunk >= 0
    s = jnp.where(valid[None, :, None, None, None, :], s, -jnp.inf)
    sink = sinks.astype(jnp.float32).reshape(ATT_KV_HEADS, ATT_GROUP)[None, None, :, :, None]
    m = jnp.maximum(s.max(axis=-1), sink)
    p = jnp.exp(s - m[..., None])
    probs = p / (p.sum(axis=-1) + jnp.exp(sink - m))[..., None]
    o = jnp.einsum('bchgqk,bckhd->bcqhgd', probs.astype(v.dtype), vb)
    return o.reshape(bsz, seq, ATT_Q_WIDTH)

def hgrn_lower_bound(lower_bounds, layer):
    lb = jnp.cumsum(jax.nn.softmax(lower_bounds.astype(jnp.float32), axis=0), axis=0)
    return lb[layer]

def hgrn2_chunkwise(q, f_logit, i, lower_bound):
    bsz, seq = q.shape[0], q.shape[1]
    n_chunks = seq // CHUNK
    f32 = jnp.float32
    lb = lower_bound.reshape(HG_HEADS, HG_KEY_DIM)
    z = f_logit.astype(f32).reshape(bsz, seq, HG_HEADS, HG_KEY_DIM)
    log_f = jnp.log(lb + (1.0 - lb) * jax.nn.sigmoid(z))
    key = (1.0 - lb) * jax.nn.sigmoid(-z)
    qf = jax.nn.silu(q.astype(f32).reshape(bsz, seq, HG_HEADS, HG_KEY_DIM))
    val = i.astype(f32).reshape(bsz, seq, HG_HEADS, HG_VAL_DIM)

    def to_chunks(t):
        return t.reshape(bsz, n_chunks, CHUNK, HG_HEADS, t.shape[-1]).transpose(1, 0, 3, 2, 4)

    causal = jnp.tril(jnp.ones((CHUNK, CHUNK), dtype=bool))

    def chunk_step(state, inp):
        qc, kc, vc, lfc = inp
        b = jnp.cumsum(lfc, axis=2)
        diff = b[:, :, :, None, :] - b[:, :, None, :, :]
        decay = jnp.exp(jnp.where(causal[:, :, None], diff, -jnp.inf))
        scores = jnp.einsum('bhtd,bhsd,bhtsd->bhts', qc, kc, decay)
        out = (jnp.einsum('bhts,bhsv->bhtv', scores, vc)
               + jnp.einsum('bhtd,bhdv->bhtv', qc * jnp.exp(b), state))
        b_last = b[:, :, -1:, :]
        new_state = (jnp.exp(b_last[:, :, 0, :])[..., None] * state
                     + jnp.einsum('bhsd,bhsv->bhdv', kc * jnp.exp(b_last - b), vc))
        return new_state, out

    state0 = jnp.zeros((bsz, HG_HEADS, HG_KEY_DIM, HG_VAL_DIM), f32)
    _, o = lax.scan(chunk_step, state0, (to_chunks(qf), to_chunks(key), to_chunks(val), to_chunks(log_f)))
    return o.transpose(1, 0, 3, 2, 4).reshape(bsz, seq, HG_HEADS, HG_VAL_DIM)

def hgrn2_output(o, g, norm_w, dtype):
    bsz, seq = o.shape[0], o.shape[1]
    on = rms_norm(o, norm_w.reshape(HG_HEADS, HG_VAL_DIM))
    gf = jax.nn.silu(g.astype(jnp.float32).reshape(bsz, seq, HG_HEADS, HG_VAL_DIM))
    return (on * gf).reshape(bsz, seq, HG_V_WIDTH).astype(dtype)

def conv_ffn(h, w_up, conv_w, conv_b, w_down):
    u = h @ w_up
    a, b = jnp.split(u, 2, axis=-1)
    a_pad = jnp.pad(a, ((0, 0), (CONV_WIDTH - 1, 0), (0, 0)))
    a = lax.conv_general_dilated(a_pad, conv_w[:, None, :], window_strides=(1,), padding='VALID',
                                 dimension_numbers=('NWC', 'WIO', 'NWC'),
                                 feature_group_count=D_FF) + conv_b
    return (jax.nn.gelu(a, approximate=True) * b) @ w_down

def setup_inputs(seed: int = 0) -> dict:
    key = jax.random.key(seed)
    ks = jax.random.split(key, 20)
    f32 = jnp.float32

    def dense(k, shape, fan_in):
        return jax.random.normal(k, shape, f32) * fan_in ** -0.5

    def gain(k, shape):
        return 1.0 + 0.02 * jax.random.normal(k, shape, f32)

    return {
        'x': jax.random.normal(ks[0], (BATCH, SEQ, D_MODEL), f32),
        'c': jax.random.normal(ks[1], (BATCH, D_MODEL), f32),
        'w_mod': dense(ks[2], (DEPTH, D_MODEL, N_MOD * D_MODEL), D_MODEL),
        'b_mod': 0.02 * jax.random.normal(ks[3], (DEPTH, N_MOD * D_MODEL), f32),
        'pre_mix_norm': gain(ks[4], (DEPTH, D_MODEL)),
        'w_in': dense(ks[5], (DEPTH, D_MODEL, IN_WIDTH), D_MODEL),
        'attn_sinks': jax.random.normal(ks[6], (DEPTH, ATT_HEADS), f32),
        'hg_lower_bounds': 0.1 * jax.random.normal(ks[7], (DEPTH + 1, HG_K_WIDTH), f32),
        'hg_out_norm': gain(ks[8], (DEPTH, HG_V_WIDTH)),
        'w_branch_a': dense(ks[9], (DEPTH, ATT_Q_WIDTH, D_MODEL), ATT_Q_WIDTH),
        'w_branch_b': dense(ks[10], (DEPTH, HG_V_WIDTH, D_MODEL), HG_V_WIDTH),
        'w_out': dense(ks[11], (DEPTH, D_MODEL, D_MODEL), D_MODEL),
        'post_mix_norm': gain(ks[12], (DEPTH, D_MODEL)),
        'pre_ffn_norm': gain(ks[13], (DEPTH, D_MODEL)),
        'w_ffn_up': dense(ks[14], (DEPTH, D_MODEL, 2 * D_FF), D_MODEL),
        'ffn_conv_w': dense(ks[15], (DEPTH, CONV_WIDTH, D_FF), CONV_WIDTH),
        'ffn_conv_b': 0.02 * jax.random.normal(ks[16], (DEPTH, D_FF), f32),
        'w_ffn_down': dense(ks[17], (DEPTH, D_FF, D_MODEL), D_FF),
        'post_ffn_norm': gain(ks[18], (DEPTH, D_MODEL)),
    }

def reference(x, c, w_mod, b_mod, pre_mix_norm, w_in, attn_sinks, hg_lower_bounds, hg_out_norm,
              w_branch_a, w_branch_b, w_out, post_mix_norm, pre_ffn_norm, w_ffn_up, ffn_conv_w,
              ffn_conv_b, w_ffn_down, post_ffn_norm):
    split_idx = [int(s) for s in np.cumsum(IN_SPLIT_SIZES)[:-1]]
    for l in range(DEPTH):
        mod = jax.nn.silu(c) @ w_mod[l] + b_mod[l]
        sh1, sc1, g1, sh2, sc2, g2 = jnp.split(mod[:, None, :], N_MOD, axis=-1)

        h = rms_norm(x, pre_mix_norm[l]) * (1.0 + sc1) + sh1
        proj = h @ w_in[l]
        q_a, k_a, v_a, f_b, q_b, i_b, g_b, gate_a, gate_b = jnp.split(proj, split_idx, axis=-1)
        y_a = sliding_window_sink_attention(q_a, k_a, v_a, attn_sinks[l]) @ w_branch_a[l]
        lb = hgrn_lower_bound(hg_lower_bounds, l)
        o_b = hgrn2_chunkwise(q_b, f_b, i_b, lb)
        y_b = hgrn2_output(o_b, g_b, hg_out_norm[l], h.dtype) @ w_branch_b[l]
        merged = jax.nn.sigmoid(gate_a) * y_a + jax.nn.sigmoid(gate_b) * y_b
        x = x + g1 * rms_norm(merged @ w_out[l], post_mix_norm[l])

        h = rms_norm(x, pre_ffn_norm[l]) * (1.0 + sc2) + sh2
        y = conv_ffn(h, w_ffn_up[l], ffn_conv_w[l], ffn_conv_b[l], w_ffn_down[l])
        x = x + g2 * rms_norm(y, post_ffn_norm[l])
    return x


_drawn_inputs = setup_inputs


def setup_inputs(seed=0):
    import zlib

    import numpy as np

    out = dict(_drawn_inputs(seed))
    spreads = {}
    factors = {'pre_mix_norm': 4.715,
     'hg_lower_bounds': 8.0,
     'hg_out_norm': 6.868,
     'post_mix_norm': 5.176,
     'pre_ffn_norm': 13.019,
     'ffn_conv_b': 44.198,
     'post_ffn_norm': 71.17}
    for name, (base, spread) in spreads.items():
        noise = np.random.default_rng([zlib.crc32(name.encode()), seed]).standard_normal(out[name].shape)
        drawn = base * np.exp(spread * noise) if base else spread * noise
        out[name] = jnp.asarray(drawn.astype(out[name].dtype))
    for name, factor in factors.items():
        out[name] = (out[name] * factor).astype(out[name].dtype)
    return out
```

```python
from contextlib import ExitStack

import numpy as np

import concourse.bass as bass
from concourse import mybir

F32 = mybir.dt.float32
F32R = mybir.dt.float32r
I32 = mybir.dt.int32
ALU = mybir.AluOpType
ACT = mybir.ActivationFunctionType
AX = mybir.AxisListType
ds = bass.ds

P = 128
T = 512
D = 2048
KT = D // P
TT = T // P
CHUNK = 64
NCH = T // CHUNK
HEADS = 8
DFF = 5504
FB = DFF // P
CONV = 3
EPS = 1e-6
NEG = -1e30
LEVELS = [32, 16, 8, 4, 2, 1]

RAW = 4
SPL = 2
PIECE = 1024

COL_Q, COL_K, COL_V, COL_F, COL_QB, COL_I, COL_G = 0, 1024, 1280, 1536, 2560, 3584, 4608
COL_GA, COL_GB = 5632, 7680
BLOCKS = (COL_Q, COL_I, COL_QB, COL_F, COL_G)
MOD_SH1, MOD_SC1, MOD_G1, MOD_SH2, MOD_SC2, MOD_G2 = (KT * n for n in range(6))

KV_PIECES = 8
HEAD_PIECES = 2 * len(BLOCKS)
P1 = KV_PIECES
P2 = P1 + HEADS * HEAD_PIECES
PAIR_PIECES = 12
P3 = P2 + KT // 2 * PAIR_PIECES
P4 = P3 + 32
P5 = P4 + 4 * FB
END = P5 + 2 * FB
MODS_HEAD = 64
PAIR_MODS = 16
N1 = KV_PIECES + MODS_HEAD
N2 = N1 + HEADS * HEAD_PIECES
N3 = N2 + KT // 2 * (PAIR_PIECES + PAIR_MODS)
N4 = N3 + 32
N5 = N4 + 4 * FB
ORD = 15
MODS_IN_STEP = [1] * 4 + [2] * 6 + [0] * 2


def block_kernel(nc, x, c, w_mod, b_mod, pre_mix_norm, w_in, attn_sinks, hg_lower_bounds, hg_out_norm,
                 w_branch_a, w_branch_b, w_out, post_mix_norm, pre_ffn_norm, w_ffn_up, ffn_conv_w,
                 ffn_conv_b, w_ffn_down, post_ffn_norm, out):
    x_rows = x.rearrange("b (i p) d -> (b i) p d", p=P)
    out_rows = out.rearrange("b (i p) d -> (b i) p d", p=P)
    kp = lambda w: w.rearrange("l (kt p) n -> p (l kt) n", p=P)
    w_mod_t, w_in_t, w_out_t, w_up_t, w_down_t = kp(w_mod), kp(w_in), kp(w_out), kp(w_ffn_up), kp(w_ffn_down)
    w_ba_t, w_bb_t = kp(w_branch_a), kp(w_branch_b)
    as_rows = lambda v: v.rearrange("l (n p) -> (l n) p", p=P)

    k_scr = nc.dram_tensor("k_scratch", [HEADS, CHUNK, T], F32, kind="Internal").ap()
    v_scr = nc.dram_tensor("v_scratch", [HEADS, TT, P, CHUNK], F32, kind="Internal").ap()
    g_scr = nc.dram_tensor("gain_scratch", [2 * KT, P], F32, kind="Internal").ap()
    x2_scr = nc.dram_tensor("x2_scratch", [TT, P, D], F32, kind="Internal").ap()

    with ExitStack() as ctx:
        sb = lambda name, shape, dt=F32: ctx.enter_context(nc.sbuf_tensor(name, shape, dt))
        sem_names = []

        def sem(name):
            sem_names.append(name)
            return ctx.enter_context(nc.semaphore(name))

        def layouts(kib, *sets):
            got = []
            for s in sets:
                assert sum(4 * int(np.prod(shape[1:])) for _, shape, _ in s) <= kib * 1024
                with ExitStack() as inner:
                    got.append({n: inner.enter_context(nc.sbuf_tensor(n, shape, dt)) for n, shape, dt in s})
            ctx.enter_context(nc.sbuf_tensor(f"region_{sem_names and len(sem_names)}_{kib}", [P, kib * 256], F32))
            return got

        RH = layouts(
            64,
            [("h_hi", [P, KT, T], F32R), ("h_lo", [P, KT, T], F32R)],
            [("x_again", [P, TT, D], F32), ("gain1", [P, D], F32)],
            [("y2", [P, TT, D], F32), ("x2_again", [P, TT, D], F32)])
        h_hi, h_lo = RH[0]["h_hi"], RH[0]["h_lo"]
        x_again, gain1 = RH[1]["x_again"], RH[1]["gain1"]
        y2, x2_again = RH[2]["y2"], RH[2]["x2_again"]
        RO = layouts(
            96,
            [("x_in", [P, TT, D], F32), ("xT", [P, KT, T], F32), ("square_junk", [P, D], F32),
             ("vec_rows", [P, 4, P], F32), ("gain_rows", [2 * KT, P], F32)],
            [("kvT", [P, 4, T], F32), ("v_nat", [P, TT, 4 * CHUNK], F32)],
            [("o_raw", [P, 2 * HEADS, T], F32),
             ("kcur", [P, 2, T], F32), ("vcur", [P, TT, P], F32), ("prob", [P, 2, TT, 256], F32),
             ("probT", [P, 2, TT, P], F32), ("qa", [P, T], F32), ("iraw", [P, T], F32), ("qh", [P, T], F32),
             ("zf", [P, T], F32), ("gh", [P, T], F32), ("key", [P, T], F32), ("cum", [P, T], F32),
             ("ex", [P, T], F32), ("rx", [P, T], F32), ("vn", [P, TT, P], F32), ("kdn", [P, TT, P], F32),
             ("dif", [P, 2, T], F32), ("eb", [P, T], F32), ("qb", [P, T], F32), ("S", [P, T], F32),
             ("state", [P, NCH, P], F32), ("xlev", [P, 2, T], F32), ("keep", [P, T], F32),
             ("lev_mask", [P, 6, CHUNK], F32), ("dist", [P, 192], F32), ("band", [P, 192], F32),
             ("bias_t", [P, 192], F32)],
            [("o_lo", [P, 2 * HEADS, T], F32R), ("o_hi", [P, 2 * HEADS, T], F32R), ("merged", [P, KT, T], F32)],
            [("y1", [P, TT, D], F32), ("m_hi", [P, KT, T], F32R), ("m_lo", [P, KT, T], F32R)],
            [("y1_kept", [P, TT, D], F32), ("m_kept", [P, KT, T], F32), ("x2_junk", [P, D], F32), ("diag", [P, TT, P], F32)],
            [("act", [P, FB, T], F32), ("gain2", [P, D], F32)])
        x_in, xT, square_junk, vec_rows = (RO[0][n] for n in ("x_in", "xT", "square_junk", "vec_rows"))
        kvT, v_nat = RO[1]["kvT"], RO[1]["v_nat"]
        L = RO[2]
        o_raw, kcur, vcur, prob, probT = (L[n] for n in ("o_raw", "kcur", "vcur", "prob", "probT"))
        qa, iraw, qh, zf, gh, key, cum = (L[n] for n in ("qa", "iraw", "qh", "zf", "gh", "key", "cum"))
        ex, rx, vn, kdn, dif, eb, qb, S = (L[n] for n in ("ex", "rx", "vn", "kdn", "dif", "eb", "qb", "S"))
        state, xlev, keep, lev_mask = (L[n] for n in ("state", "xlev", "keep", "lev_mask"))
        dist, band, bias_t = (L[n] for n in ("dist", "band", "bias_t"))
        gtmps = [kdn[:, 2 * i:2 * i + 2, :].rearrange("p a b -> p (a b)") for i in range(2)]
        o_lo, o_hi, merged = (RO[3][n] for n in ("o_lo", "o_hi", "merged"))
        y1, m_hi, m_lo = RO[4]["y1"], RO[4]["m_hi"], RO[4]["m_lo"]
        x2_junk, diag = RO[5]["x2_junk"], RO[5]["diag"]
        act_t, gain2 = RO[6]["act"], RO[6]["gain2"]
        raw = [sb(f"raw{i}", [P, PIECE]) for i in range(RAW)]
        w_hi = [sb(f"w_hi{i}", [P, PIECE], F32R) for i in range(SPL)]
        w_lo = [sb(f"w_lo{i}", [P, PIECE], F32R) for i in range(SPL)]
        RS = layouts(
            8,
            [("small", [P, 4, T], F32)],
            [("a_lo", [P, 2, T], F32R), ("a_hi", [P, 2, T], F32R)])
        small = RS[0]["small"]
        a_hi, a_lo = RS[1]["a_hi"], RS[1]["a_lo"]
        acc = sb("acc", [P, T])
        ident = sb("ident", [P, P])
        ones = sb("ones", [P, P])
        vec = sb("vec", [P, 4, P])
        modc = sb("modc", [P, 6 * KT])
        csil = sb("csil", [P, KT])
        a1 = sb("a1", [P, 2, KT])
        gcol = sb("gcol", [P, 2, KT])
        lbc = sb("lbc", [P, 6, HEADS])
        slope = sb("slope", [P, 2 * HEADS])
        sink = sb("sink", [P, 2 * HEADS])
        st = sb("st", [P, 64])
        eps_c = st[:, 0:1]
        ssq = st[:, 4:8]
        rms = st[:, 8:12]
        ssg = st[:, 16:32]
        smx = [st[:, 32 + 4 * e:36 + 4 * e] for e in range(2)]
        den = [st[:, 40 + 4 * e:44 + 4 * e] for e in range(2)]
        esk = [st[:, 48 + 4 * e:52 + 4 * e] for e in range(2)]
        ssq2 = st[:, 56:60]
        rms2 = st[:, 60:64]

        bmod_c, c_c, pre_mix_c = vec[:, 0, 0:96], vec[:, 0, 96:112], vec[:, 0, 112:128]
        pre_ffn_c, post_mix_c, post_ffn_c = (vec[:, 1, 16 * n:16 * n + 16] for n in range(3))
        bound_c, hgn_c, convb_c = vec[:, 1, 48:64], vec[:, 1, 64:72], vec[:, 1, 72:72 + FB]
        tap_c = [vec[:, 2, 0:FB], vec[:, 2, FB:2 * FB], vec[:, 3, 0:FB]]

        ps = lambda name, shape: ctx.enter_context(nc.psum_tensor(name, shape, F32))
        A = [ps(f"acc_bank{i}", [P, T]) for i in range(3)]
        SC = ps("two_banks", [P, 2 * T])
        SC0, SC1 = SC[:, 0:T], SC[:, T:2 * T]
        TA, TB, PB = ps("bank_ta", [P, T]), ps("bank_tb", [P, T]), ps("bank_pb", [P, T])
        KV_BANKS = [A[0], A[1], A[2], PB]
        OUT_BANKS = [[A[0][:], A[1][:], A[2][:], PB[:]], [SC0, SC1, TA[:], TB[:]]]
        TURN_BANKS = [TA[:], TB[:]]
        TURN4 = [SC0, SC1, TA[:], TB[:]]
        DOWN_BANKS = [A[0][:], A[1][:], A[2][:], PB[:], SC0, SC1, TA[:], TB[:]]

        landed = [sem(f"raw_landed{i}") for i in range(RAW)]
        hi_ready, lo_ready = sem("hi_ready"), sem("lo_ready")
        multiplied = sem("multiplied")
        mod_ops = sem("mod_ops")
        vec_landed, x_landed = sem("vec_landed"), [sem(f"x_landed{i}") for i in range(TT)]
        consts_ready, pool_order = sem("consts_ready"), sem("pool_order")
        setup_dve = sem("setup_dve")
        vec_turned, vec_ready = sem("vec_turned"), sem("vec_ready")
        c_exp = sem("c_exp")
        ssq_ready, root_ready, rms_ready, xn_ready = sem("ssq_ready"), sem("root_ready"), sem("rms_ready"), sem("xn_ready")
        x_turned, xT_ready = sem("x_turned"), sem("xT_ready")
        mod_summed, mod_taken, cols_ready = sem("mod_summed"), sem("mod_taken"), sem("cols_ready")
        hx_ready, hh_ready, h_ready = sem("hx_ready"), sem("hh_ready"), sem("h_ready")
        bounds_exp, bounds_ready, bounds_in = sem("bounds_exp"), sem("bounds_ready"), sem("bounds_in")
        kv_out, v_turned, v_ready, kv_stored = sem("kv_out"), sem("v_turned"), sem("v_ready"), sem("kv_stored")
        temps_ready = sem("temps_ready")
        names = ("qa_ready i_ready q_ready z_ready g_ready kcur_landed vcur_landed vT_done vn_ready scores "
                 "s_taken negmax p_exp prob pT pT_own pT_prev "
                 "pv pv_out ez_ready rz_ready lf_ready key_ready cum_ready eq_ready rq_ready "
                 "eg_ready gs_ready eb_ready qb_ready kd_ready kdT_done kdn_ready U_done diag_done S_ready "
                 "oT_done sq_ready ss_done o_ln r_ready "
                 "o_part o_scaled o_ready").split()
        E = {n: sem(n) for n in names}
        dif_ready = sem("dif_ready")
        fac_ready = sem("fac_ready")
        xl_ready = sem("xl_ready")
        lev_done = sem("lev_done")
        lev_masked, lev_kept = sem("lev_masked"), sem("lev_kept")
        d_order = sem("d_order")
        o_hi_ready, o_split = sem("o_hi_ready"), sem("o_split")
        gate_ready, ga_used, merged_ready = sem("gate_ready"), sem("ga_used"), sem("merged_ready")
        mh_ready, m_split = sem("mh_ready"), sem("m_split")
        gcol_ready, gcol_turned, grow_ready, grow_stored = sem("gcol_ready"), sem("gcol_turned"), sem("grow_ready"), sem("grow_stored")
        gain1_landed, x3_landed = sem("gain1_landed"), sem("x3_landed")
        y1_out, y1_sq = sem("y1_out"), sem("y1_sq")
        x2_ready, x2_sq, x2_root, x2_rms, diag_ready, x2_stored = (sem(n) for n in ("x2_ready", "x2_sq", "x2_root", "x2_rms", "diag_ready", "x2_stored"))
        h2_turned, h2x, h2h, h2_ready = sem("h2_turned"), sem("h2x"), sem("h2h"), sem("h2_ready")
        conv_step, gelu_ready, act_ready = sem("conv_step"), sem("gelu_ready"), sem("act_ready")
        gain2_landed, x2b_landed = sem("gain2_landed"), sem("x2b_landed")
        ah_ready, al_ready = sem("ah_ready"), sem("al_ready")
        y_done, y2_out, y2_sq = sem("y_done"), sem("y2_out"), sem("y2_sq")
        y_sum, y_root, out_ready, out_stored = (sem(n) for n in ("y_sum", "y_root", "out_ready", "out_stored"))

        def both(v, e):
            return v * 2 + (e - 1)

        def level(v, u, n):
            return v * n + (u - 6)

        def chunk_sum(ch):
            lo = (ch % 2) * T + (ch // 2) * P
            return SC[:, lo:lo + P]

        def piece(buf, kt):
            return buf[:].rearrange("p (k n) -> p k n", k=kt)

        def kv_pos(g):
            if g >= KV_PIECES - 2:
                return N1 - KV_PIECES + g
            return 24 + 9 * g

        def pair_order():
            items, m = [("w", 0)], 0
            for k in range(PAIR_PIECES):
                if k + 1 < PAIR_PIECES:
                    items.append(("w", k + 1))
                for _ in range(MODS_IN_STEP[k]):
                    items.append(("m", m))
                    m += 1
            return items
        PAIR = pair_order()
        PAIR_POS = {it: n for n, it in enumerate(PAIR)}

        def mod_bank(n):
            return SC1 if n < 8 and n % 2 else SC0

        SC1_SUMS = [acc[:], small[:, 1, :]]
        SH1_SUMS = [small[:, 0, :], square_junk[:, 0:T]]

        block = ctx.enter_context(nc.Block())

        @block.sync
        def _(sp):
            last = [None] * RAW

            def load(n, it, kind, idx, idx_per, src, looped=()):
                slot = n % RAW
                if not isinstance(src, bass.AP):
                    build, start = src
                    src = build(start)
                if last[slot] is not None:
                    sp.wait_ge(*last[slot])
                for s, v in looped:
                    sp.wait_ge(s, v)
                kt = src.shape[1]
                dst = piece(raw[slot], kt)
                sp.dma_start(dst, src).then_inc(landed[slot], 16)
                if kind == "w":
                    last[slot] = (lo_ready, idx + it * idx_per + 1)
                else:
                    last[slot] = (mod_ops, (idx + it * idx_per + 1) * 2)

            def run(n0, passes, items, srcs, early=None):
                per = len(items)
                assert per % RAW == 0
                before = list(last)
                with sp.Fori(1, passes + 1) as turn:
                    it = turn - 1
                    for slot in range(RAW):
                        last[slot] = None
                    for n, (kind, idx, ip) in enumerate(items):
                        looped = []
                        if n < RAW:
                            if before[(n0 + n) % RAW] is not None:
                                looped.append(before[(n0 + n) % RAW])
                            pk, pi, pp = items[n - RAW]
                            v = pi - pp + 1
                            looped.append((lo_ready, it * pp + v) if pk == "w" else (mod_ops, (it * pp + v) * 2))
                        if early is not None and n + 1 == early:
                            slot = (n0 + early) % RAW
                            looped.append(last[slot])
                            last[slot] = None
                        load(n0 + n, it, kind, idx, ip, srcs(it, n), looped)
                for n in range(per - RAW, per):
                    kind, idx, ip = items[n]
                    v = idx + (passes - 1) * ip + 1
                    last[(n0 + n) % RAW] = (lo_ready, v) if kind == "w" else (mod_ops, 2 * v)

            for dst, src in (
                    (vec_rows[0:96, 0, :], as_rows(b_mod)), (vec_rows[96:112, 0, :], as_rows(c)),
                    (vec_rows[112:128, 0, :], as_rows(pre_mix_norm)), (vec_rows[0:16, 1, :], as_rows(pre_ffn_norm)),
                    (vec_rows[16:32, 1, :], as_rows(post_mix_norm)), (vec_rows[32:48, 1, :], as_rows(post_ffn_norm)),
                    (vec_rows[48:64, 1, :], as_rows(hg_lower_bounds)), (vec_rows[64:72, 1, :], as_rows(hg_out_norm)),
                    (vec_rows[72:72 + FB, 1, :], as_rows(ffn_conv_b)),
                    (vec_rows[0:2 * FB, 2, :], ffn_conv_w.rearrange("l t (n p) -> (l t n) p", p=P)[0:2 * FB]),
                    (vec_rows[0:FB, 3, :], ffn_conv_w.rearrange("l t (n p) -> (l t n) p", p=P)[2 * FB:3 * FB]),
                    (sink[:], attn_sinks.partition_broadcast(P).rearrange("q l n -> q (l n)"))):
                sp.dma_start(dst, src).then_inc(vec_landed, 16)

            def load_kv(g):
                load(kv_pos(g), 0, "w", g, 0, w_in_t[:, 2 * g:2 * g + 2, COL_K:COL_K + 512])

            n, m, g = 0, 0, 0
            for ch in range(4):
                for base in (MOD_SC1, MOD_SH1):
                    col = base * P + ch * 512
                    if m == 0:
                        for i in range(8):
                            load(n + i, 0, "m", m + i, 0, w_mod_t[:, 2 * i:2 * i + 2, col:col + 512])
                    else:
                        run(n, 2, [("m", m + i, 4) for i in range(4)],
                            lambda it, i, col=col: (lambda r: w_mod_t[:, ds(r, 2), col:col + 512], it * 8 + 2 * i))
                    n, m = n + 8, m + 8
                    if ch:
                        load_kv(g)
                        n, g = n + 1, g + 1
            for g in (KV_PIECES - 2, KV_PIECES - 1):
                load_kv(g)

            def head_src(h, i):
                b, half = divmod(i, 2)
                return (lambda r: w_in_t[:, half * 8:half * 8 + 8, ds(r, P)]), h * P + BLOCKS[b]
            run(N1, HEADS // 2, [("w", P1 + i, 2 * HEAD_PIECES) for i in range(2 * HEAD_PIECES)],
                lambda it, i: head_src(it * 2 + i // HEAD_PIECES, i % HEAD_PIECES))

            def pair_src(it, i):
                kind, k = PAIR[i]
                if kind == "m":
                    pc, kk = divmod(k, 8)
                    return (lambda r: w_mod_t[:, 2 * kk:2 * kk + 2, ds(r, 512)]), it * 1024 + (MOD_G1 * P + pc * 512)
                if k < 8:
                    r, j = divmod(k // 2, 2)
                    return (lambda q: w_in_t[:, (k % 2) * 8:(k % 2) * 8 + 8, ds(q, P)]), it * 256 + ((COL_GA, COL_GB)[r] + j * P)
                r, j = divmod(k - 8, 2)
                return (lambda q: (w_ba_t, w_bb_t)[r][:, :, ds(q, P)]), it * 256 + j * P
            run(N2, KT // 2, [("w", P2 + k, PAIR_PIECES) if kind == "w" else ("m", MODS_HEAD + k, PAIR_MODS)
                                 for kind, k in PAIR], pair_src, PAIR_POS[("w", 8)])
            run(N3, 4, [("w", P3 + i, 8) for i in range(8)],
                lambda it, i: (lambda r: w_out_t[:, 2 * i:2 * i + 2, ds(r, 512)], it * 512))
            run(N4, FB, [("w", P4 + i, 4) for i in range(4)],
                lambda it, i: (lambda r: w_up_t[:, (i % 2) * 8:(i % 2) * 8 + 8, ds(r, P)], it * P + (i // 2) * DFF))
            for s in range(2):
                base = s * FB
                for i in range(3):
                    load(N5 + base + i, 0, "w", P5 + base + i, 0, w_down_t[:, i:i + 1, s * 1024:s * 1024 + 1024])
                run(N5 + base + 3, (FB - 3) // 4, [("w", P5 + base + 3 + i, 4) for i in range(4)],
                    lambda it, i, s=s: (lambda r: w_down_t[:, ds(r, 1), s * 1024:s * 1024 + 1024], it * 4 + (3 + i)))
            for i in range(TT):
                sp.wait_ge(out_ready, i + 1)
                sp.dma_start(out_rows[i], y2[:, i, :]).then_inc(out_stored, 16)
            sp.wait_ge(out_stored, 16 * TT)

        def split_hi(act, g, n, it=0, gp=0, np_=0):
            act.wait_ge(landed[n % RAW], 16 * (n // RAW + 1) + it * (16 * (np_ // RAW)))
            if g >= SPL or gp:
                act.wait_ge(multiplied, g - SPL + 1 + it * gp)
            act.copy(w_hi[g % SPL][:], raw[n % RAW][:]).then_inc(hi_ready, 1)

        def split_lo(dve, g, n, it=0, gp=0):
            dve.wait_ge(hi_ready, g + 1 + it * gp)
            dve.tensor_tensor(w_lo[g % SPL][:], raw[n % RAW][:], w_hi[g % SPL][:].bitcast(F32),
                              ALU.subtract).then_inc(lo_ready, 1)

        def level_view(t, m):
            return t.rearrange("p (n two m) -> p n two m", two=2, m=m)

        def bank_complete(eng, s, b):
            if b < 7:
                eng.wait_ge(y_done, 7 * s + b + 1)
            else:
                eng.wait_ge(multiplied, P5 + (s + 1) * FB)

        def sweep_out_act(act, s, banks=range(8)):
            for b in banks:
                bank_complete(act, s, b)
                act.wait_ge(y2_sq, 8 * s + b)
                act.activation(acc[:], DOWN_BANKS[b], ACT.Square,
                               accum_out=ssg[:, (b // 2) * 4 + 2 * s + b % 2:(b // 2) * 4 + 2 * s + b % 2 + 1]).then_inc(y2_sq, 1)

        @block.tensor
        def _(pe):
            def three(o, stat, mov, start, stop):
                pe.matmul(o, stat[0], mov[0], start=start, stop=False)
                pe.matmul(o, stat[0], mov[1], start=False, stop=False)
                return pe.matmul(o, stat[1], mov[0], start=False, stop=stop)

            def weights(g, kt):
                return piece(w_hi[g % SPL], kt), piece(w_lo[g % SPL], kt)

            def block_piece(g, it, gp, o, mov_hi, mov_lo, k0, first, last, operand=None):
                pe.wait_ge(lo_ready, g + 1 + it * gp)
                wh, wl = weights(g, 8)
                for k in range(8):
                    if operand is not None:
                        pe.wait_ge(operand, k0 + k + 1)
                    mm = three(o, (wh[:, k, :], wl[:, k, :]), (mov_hi[:, k0 + k, :], mov_lo[:, k0 + k, :]),
                               first and k == 0, last and k == 7)
                mm.then_inc(multiplied, 1)

            pe.wait_ge(vec_landed, 12 * 16)
            pe.wait_ge(consts_ready, 1)
            for j, rows in enumerate((P, 72 + FB, 2 * FB, FB)):
                t = pe.transpose(SC1[:, j * P:j * P + rows], vec_rows[0:rows, j, :], ident[0:rows, 0:rows])
            t.then_inc(vec_turned, 1)
            def mod_sum(piece_no, sums, it=0, ip=0):
                pe.wait_ge(mod_ops, 16 * (piece_no + 1) + it * (16 * ip))
                bank = mod_bank(piece_no)
                taken = piece_no if ip else max(piece_no - 1, 0)
                if taken:
                    pe.wait_ge(mod_taken, taken + it * ip)
                for j in range(4):
                    for src in sums:
                        t = pe.matmul(bank[:, j:j + 1], src[:, j * P:(j + 1) * P], ones[:, 0:1],
                                      start=src is sums[0], stop=src is sums[-1])
                t.then_inc(mod_summed, 1)

            mod_sum(0, SC1_SUMS)
            pe.wait_ge(xn_ready, TT)
            for kb in range(KT):
                if kb == 7:
                    mod_sum(1, SH1_SUMS)
                if kb >= 2:
                    pe.wait_ge(xT_ready, kb - 1)
                for i in range(TT):
                    t = pe.transpose(TURN_BANKS[kb % 2][:, i * P:(i + 1) * P], x_in[:, i, kb * P:(kb + 1) * P], ident[:])
                t.then_inc(x_turned, 1)

            def kv_piece(g):
                pe.wait_ge(h_ready, 4 * (g // 2) + 4)
                pe.wait_ge(lo_ready, g + 1)
                wh, wl = weights(g, 2)
                for k in range(2):
                    kb = 2 * g + k
                    for b in range(4):
                        mm = three(KV_BANKS[b][:], (wh[:, k, b * P:(b + 1) * P], wl[:, k, b * P:(b + 1) * P]),
                                   (h_hi[:, kb, :], h_lo[:, kb, :]), kb == 0, kb == KT - 1)
                mm.then_inc(multiplied, 1)

            for ch in range(1, 4):
                mod_sum(2 * ch, SC1_SUMS)
                kv_piece(2 * ch - 2)
                mod_sum(2 * ch + 1, SH1_SUMS)
                kv_piece(2 * ch - 1)
            kv_piece(KV_PIECES - 2)
            kv_piece(KV_PIECES - 1)
            pe.wait_ge(kv_out, 4)
            for i in range(TT):
                for b in range(2):
                    t = pe.transpose(TURN4[i][:, b * P:(b + 1) * P], kvT[:, 2 + b, i * P:(i + 1) * P], ident[:])
            t.then_inc(v_turned, 1)

            def mix(step, v, first=False):
                if step == 0:
                    pe.wait_ge(E["i_ready"], v)
                    pe.wait_ge(lev_kept, level(v - 1, 6, 6))
                    if first:
                        pe.wait_ge(v_ready, 4)
                        pe.wait_ge(temps_ready, 1)
                    for i in range(TT):
                        t = pe.transpose(TA[:, i * P:(i + 1) * P], iraw[:, i * P:(i + 1) * P], ident[:])
                    t.then_inc(E["vT_done"], 1)
                    scores(0, v)
                elif step == 1:
                    pe.wait_ge(E["s_taken"], both(v, 0))
                    scores(1, v)
                elif step == 2:
                    turn_probs(0, v)
                elif step == 3:
                    attend(0, v)
                    turn_probs(1, v)
                elif step == 4:
                    attend(1, v)
                    pe.wait_ge(E["pT_own"], both(v, 1))
                    pe.wait_ge(E["kd_ready"], v)
                    for i in range(TT):
                        t = pe.transpose(TA[:, i * P:(i + 1) * P], dif[:, 0, i * P:(i + 1) * P], ident[:])
                    t.then_inc(E["kdT_done"], 1)
                elif step == 5:
                    pe.wait_ge(E["kdn_ready"], v)
                    pe.wait_ge(E["s_taken"], both(v, 1))
                    for ch in range(NCH):
                        lo = CHUNK * (ch % 2)
                        t = pe.matmul(chunk_sum(ch), kdn[lo:lo + CHUNK, ch // 2, :],
                                      vn[lo:lo + CHUNK, ch // 2, :], start=True, stop=True)
                    t.then_inc(E["U_done"], 1)
                    pe.wait_ge(E["pT_prev"], both(v, 1))
                    for i in range(TT):
                        t = pe.matmul(TB[:, i * P:(i + 1) * P], key[:, i * P:(i + 1) * P], qh[:, i * P:(i + 1) * P],
                                      start=True, stop=True)
                    t.then_inc(E["diag_done"], 1)
                elif step in (6, 7, 8):
                    for u in (2 * step - 11, 2 * step - 10):
                        m = LEVELS[u - 1]
                        bank = (TA, TB)[u % 2]
                        pe.wait_ge(xl_ready, level(v, u, 6))
                        if u == 1:
                            pe.wait_ge(E["S_ready"], v)
                        elif u == 2:
                            pe.wait_ge(E["kdn_ready"], v)
                        else:
                            pe.wait_ge(lev_kept, level(v, u - 2, 6))
                        xv = level_view(xlev[:, u % 2, :], m)
                        nb = CHUNK // m
                        for i in range(TT):
                            t = pe.matmul(bank[:, i * CHUNK:(i + 1) * CHUNK], xlev[:, u % 2, i * P:(i + 1) * P],
                                          xv[:, i * nb:(i + 1) * nb, 1, :], start=True, stop=True)
                        t.then_inc(lev_done, 1)
                elif step == 9:
                    pe.wait_ge(lev_kept, level(v, 6, 6))
                    pe.wait_ge(E["pv_out"], both(v, 1))
                    for i in range(TT):
                        for ch in (2 * i, 2 * i + 1):
                            pe.matmul(PB[:, ch * CHUNK:(ch + 1) * CHUNK], state[:, ch, :],
                                      qb[:, ch * CHUNK:(ch + 1) * CHUNK], start=ch % 2 == 0, stop=False)
                        t = pe.matmul(PB[:, i * P:(i + 1) * P], vn[:, i, :], S[:, i * P:(i + 1) * P], start=False, stop=True)
                    t.then_inc(E["oT_done"], 1)
                else:
                    pe.wait_ge(E["sq_ready"], v)
                    pe.matmul(TB[:], ones[:], dif[:, 1, :], start=True, stop=True).then_inc(E["ss_done"], 1)

            def scores(e, v):
                pe.wait_ge(E["qa_ready"], v)
                pe.wait_ge(E["kcur_landed"], v * 32)
                if e == 0:
                    pe.wait_ge(d_order, (v - 1) * ORD)
                for i in range(TT):
                    k0 = 0 if i == 0 else 64 * (2 * i - 1)
                    width = P if i == 0 else 192
                    t = pe.matmul(SC[:, i * 256 + 256 - width:(i + 1) * 256], qa[:, i * P:(i + 1) * P],
                                  kcur[:, e, k0:k0 + width], start=True, stop=True)
                t.then_inc(E["scores"], 1)

            def turn_probs(e, v):
                pe.wait_ge(E["prob"], both(v, e))
                if e == 0:
                    pe.wait_ge(E["r_ready"], v - 1)
                    pe.wait_ge(E["vn_ready"], v)
                else:
                    pe.wait_ge(E["pT_own"], both(v, 0))
                    pe.wait_ge(E["pT_prev"], both(v, 0))
                for i in range(TT):
                    t = pe.transpose(TA[:, i * P:(i + 1) * P], prob[:, e, i, P:2 * P], ident[:])
                for i in range(1, TT):
                    t = pe.transpose(TB[:, (i - 1) * P:i * P], prob[:, e, i, 0:P], ident[:])
                t.then_inc(E["pT"], 1)

            def attend(e, v):
                pe.wait_ge(E["pT_own"], both(v, e))
                pe.wait_ge(E["pT_prev"], both(v, e))
                pe.wait_ge(E["vcur_landed"], v * 32)
                if e == 0:
                    pe.wait_ge(E["vn_ready"], v)
                    pe.wait_ge(E["o_ready"], v - 1)
                else:
                    pe.wait_ge(E["pv_out"], both(v, 0))
                for i in range(TT):
                    t = pe.matmul(PB[:, i * P:(i + 1) * P], vcur[:, i, :], probT[:, 0, i, :], start=True, stop=i == 0)
                    if i:
                        t = pe.matmul(PB[:, i * P:(i + 1) * P], vcur[:, i - 1, :], probT[:, 1, i - 1, :],
                                      start=False, stop=True)
                t.then_inc(E["pv"], 1)

            def free_bank(b, h):
                if b < 3:
                    s, v = (("z_ready", h), ("g_ready", h), ("q_ready", h))[b]
                else:
                    s, v = (("qa_ready", h + 1), ("i_ready", h + 1))[b - 3]
                pe.wait_ge(E[s], v)

            def head_step(h, base, it, mixing, first=False):
                for k in range(HEAD_PIECES):
                    if mixing:
                        mix(k, h, first)
                    b = k // 2
                    if k % 2 == 0 and (mixing or b > 2):
                        free_bank(b, h)
                    block_piece(base + k, it, 2 * HEAD_PIECES, A[b % 3][:], h_hi, h_lo, 8 * (k % 2), k % 2 == 0, k % 2 == 1)
                if mixing:
                    mix(HEAD_PIECES, h)

            head_step(0, P1, 0, False)
            head_step(1, P1 + HEAD_PIECES, 0, True, first=True)
            with pe.Fori(0, 3) as it:
                for r in range(2):
                    head_step(it * 2 + (2 + r), P1 + (2 + r) * HEAD_PIECES, it, True)

            def pair(it, peeled):
                base = P2
                banks = [A[0], A[1], A[2], A[0], A[1], A[2], A[0], A[1]]
                for k in range(PAIR_PIECES):
                    if peeled and k < HEAD_PIECES:
                        mix(k, HEADS)
                        if k == HEAD_PIECES - 1:
                            mix(HEAD_PIECES, HEADS)
                    if k == 6:
                        if peeled:
                            pe.wait_ge(d_order, ORD * HEADS - 2)
                        mod_sum(8, [acc[:]], it, 2)
                    if k == 11:
                        mod_sum(9, [acc[:]], it, 2)
                    if k < 8:
                        q = k // 2
                        if k % 2 == 0:
                            if q == 3:
                                pe.wait_ge(gate_ready, 1 + 4 * it)
                            elif peeled:
                                pe.wait_ge(E[("z_ready", "g_ready", "q_ready")[q]], HEADS)
                            elif q == 0:
                                pe.wait_ge(ga_used, 4 * it - 1)
                            elif q == 1:
                                pe.wait_ge(ga_used, 4 * it)
                        block_piece(base + k, it, PAIR_PIECES, banks[q][:], h_hi, h_lo, 8 * (k % 2), k % 2 == 0, k % 2 == 1)
                    else:
                        pe.wait_ge(gate_ready, 4 * it + (2, 3, 4, 4)[k - 8])
                        if k == 11:
                            pe.wait_ge(ga_used, 4 * it + 1)
                        block_piece(base + k, it, PAIR_PIECES, banks[k - 4][:],
                                    o_hi, o_lo, (k - 8) // 2 * 8, True, True, o_split if peeled and k in (8, 10) else None)

            pair(0, True)
            with pe.Fori(1, KT // 2) as it:
                pair(it, False)
            pe.wait_ge(gcol_ready, 1)
            pe.transpose(SC1[0:2 * KT, 0:P], gcol[:].rearrange("p a b -> p (a b)"), ident[:]).then_inc(gcol_turned, 1)

            def out_group(g0, it, banks_free, bank_set):
                for i in range(8):
                    g = g0 + i
                    pe.wait_ge(lo_ready, g + 1 + it * 16)
                    if i == 0:
                        banks_free()
                    wh, wl = weights(g, 2)
                    for k in range(2):
                        kb = 2 * i + k
                        pe.wait_ge(m_split, kb + 1)
                        for t4 in range(TT):
                            mm = three(OUT_BANKS[bank_set][t4], (m_hi[:, kb, t4 * P:(t4 + 1) * P], m_lo[:, kb, t4 * P:(t4 + 1) * P]),
                                       (wh[:, k, :], wl[:, k, :]), kb == 0, kb == KT - 1)
                    mm.then_inc(multiplied, 1)

            with pe.Fori(0, 2) as it:
                def even_free():
                    pe.wait_ge(ga_used, 2 * KT)
                    pe.wait_ge(y1_out, it * 4 + 1)
                def odd_free():
                    pe.wait_ge(mod_taken, 24)
                    pe.wait_ge(grow_ready, 1)
                    pe.wait_ge(y1_out, it * 8 + 1)
                out_group(P3, it, even_free, 0)
                out_group(P3 + 8, it, odd_free, 1)

            pe.wait_ge(y1_out, 17)
            def turn_scaled(kb, i):
                return pe.matmul(TURN4[kb % 4][:, i * P:(i + 1) * P], y1[:, i, kb * P:(kb + 1) * P], diag[:, i, :],
                                 start=True, stop=True)

            for i in range(TT):
                pe.wait_ge(diag_ready, i + 1)
                for kb in range(4):
                    t = turn_scaled(kb, i)
                    if i == TT - 1:
                        t.then_inc(h2_turned, 1)
            for kb in range(4, KT):
                pe.wait_ge(h2x, kb - 3)
                for i in range(TT):
                    t = turn_scaled(kb, i)
                t.then_inc(h2_turned, 1)

            def up(it, peeled):
                for k in range(4):
                    if k % 2 == 0 and not peeled:
                        if k == 0:
                            pe.wait_ge(conv_step, it * 3)
                        else:
                            pe.wait_ge(act_ready, it)
                    block_piece(P4 + k, it, 4, A[k // 2][:], h_hi, h_lo, 8 * (k % 2), k % 2 == 0, k % 2 == 1,
                                h2_ready if peeled and k < 2 else None)
            up(0, True)
            with pe.Fori(1, FB) as it:
                up(it, False)

            def down(u, it, sweep, first, last):
                g = P5 + u
                pe.wait_ge(lo_ready, g + 1 + it * 4)
                pe.wait_ge(al_ready, u + 1 + it * 4)
                wh, wl = weights(g, 1)
                s = u % 2
                for b in range(8):
                    if first:
                        if sweep == 0:
                            if b < 2:
                                pe.wait_ge((conv_step, act_ready)[b], (3 * FB, FB)[b])
                        else:
                            pe.wait_ge(y2_out, b + 1)
                    t4, ch = divmod(b, 2)
                    mm = three(DOWN_BANKS[b], (a_hi[:, s, t4 * P:(t4 + 1) * P], a_lo[:, s, t4 * P:(t4 + 1) * P]),
                               (wh[:, 0, ch * 512:(ch + 1) * 512], wl[:, 0, ch * 512:(ch + 1) * 512]), first, last)
                    if last and b < 7:
                        mm.then_inc(y_done, 1)
                mm.then_inc(multiplied, 1)

            for sweep in range(2):
                base = sweep * FB
                for u in range(3):
                    down(base + u, 0, sweep, u == 0, False)
                with pe.Fori(0, 9) as it:
                    for i in range(4):
                        down(base + 3 + i, it, sweep, False, False)
                for u in range(39, 43):
                    down(base + u, 0, sweep, False, u == 42)

        @block.scalar
        def _(act):
            A_ = act.activation
            for i in range(TT):
                act.dma_start(x_in[:, i, :], x_rows[i]).then_inc(x_landed[i], 16)
            act.wait_ge(vec_ready, 1)
            A_(csil[:], c_c, ACT.Exp, scale=-1.0).then_inc(c_exp, 1)
            act.wait_ge(bounds_in, 1)
            A_(lbc[:, 2:4, :].rearrange("p a b -> p (a b)"), lbc[:, 0:2, :].rearrange("p a b -> p (a b)"), ACT.Exp).then_inc(bounds_exp, 1)
            for i in range(TT):
                act.wait_ge(x_landed[i], 16)
                act.wait_ge(ssq_ready, i)
                A_(square_junk[:], x_in[:, i, :], ACT.Square, accum_out=ssq[:, i:i + 1]).then_inc(ssq_ready, 1)
            act.wait_ge(ssq_ready, TT)
            act.wait_ge(consts_ready, 1)
            A_(rms, ssq, ACT.Sqrt, scale=1.0 / D, bias=eps_c).then_inc(root_ready, 1)
            act.wait_ge(rms_ready, 1)
            for i in range(TT):
                A_(x_in[:, i, :], x_in[:, i, :], ACT.Copy, scale=rms[:, i:i + 1]).then_inc(xn_ready, 1)
            for kb in range(KT):
                act.wait_ge(x_turned, kb + 1)
                act.copy(xT[:, kb, :], TURN_BANKS[kb % 2]).then_inc(xT_ready, 1)

            def modulate(kb):
                if kb >= 2:
                    act.wait_ge(h_ready, kb - 1)
                hx = small[:, 2 + kb % 2, :]
                A_(hx, xT[:, kb, :], ACT.Identity, scale=a1[:, 0, kb:kb + 1], bias=modc[:, MOD_SH1 + kb:MOD_SH1 + kb + 1]
                   ).then_inc(hx_ready, 1)
                act.wait_ge(hx_ready, kb + 1)
                act.copy(h_hi[:, kb, :], hx).then_inc(hh_ready, 1)

            act.wait_ge(xT_ready, KT)
            for ch in range(4):
                act.wait_ge(cols_ready, ch + 1)
                for b in range(4):
                    modulate(4 * ch + b)
                for g in (2 * ch, 2 * ch + 1):
                    split_hi(act, g, kv_pos(g))
            act.wait_ge(multiplied, KV_PIECES)
            for b in range(4):
                act.copy(kvT[:, b, :], KV_BANKS[b][:]).then_inc(kv_out, 1)
            act.wait_ge(v_turned, 1)
            for i in range(TT):
                act.copy(v_nat[:, i, :], TURN4[i][:, 0:2 * P]).then_inc(v_ready, 1)

            def exp_scores(e, v):
                act.wait_ge(E["negmax"], both(v, e))
                for i in range(TT):
                    lo = P if i == 0 else CHUNK
                    A_(prob[:, e, i, lo:256], prob[:, e, i, lo:256], ACT.Exp, bias=smx[e][:, i:i + 1],
                       accum_out=den[e][:, i:i + 1])
                A_(esk[e], smx[e], ACT.Exp, bias=sink[:, ds(v * 2 + (e - 2), 1)]).then_inc(E["p_exp"], 1)

            def factor(u, v):
                act.wait_ge(dif_ready, level(v, u, 7))
                A_(dif[:, u % 2, :], dif[:, u % 2, :], ACT.Exp).then_inc(fac_ready, 1)

            def take_prev(e, v):
                act.wait_ge(E["pT"], both(v, e))
                if e == 1:
                    act.wait_ge(E["pv"], both(v, 0))
                else:
                    act.wait_ge(E["pv"], both(v - 1, 1))
                act.copy(probT[:, 1, 0:3, :].rearrange("p a b -> p (a b)"), TB[:, 0:3 * P]).then_inc(E["pT_prev"], 1)

            def take_pv(e, v):
                act.wait_ge(E["pv"], both(v, e))
                lo = CHUNK * e
                act.copy(o_raw[lo:lo + CHUNK, ds(v - 1, 1), :].rearrange("p a b -> p (a b)"), PB[lo:lo + CHUNK, :]
                         ).then_inc(E["pv_out"], 1)

            def attention_first(k, v):
                if k == 2:
                    take_prev(0, v)
                else:
                    take_pv(0, v)
                    take_prev(1, v)

            def mix(step, v):
                if step == 0:
                    act.wait_ge(E["z_ready"], v)
                    A_(ex[:], zf[:], ACT.Exp, scale=-1.0).then_inc(E["ez_ready"], 1)
                    act.wait_ge(E["vT_done"], v)
                    act.wait_ge(E["oT_done"], v - 1)
                    act.copy(vn[:].rearrange("p a b -> p (a b)"), TA[:]).then_inc(E["vn_ready"], 1)
                    act.wait_ge(E["o_ready"], v - 1)
                    act.copy(gh[:], A[1][:]).then_inc(E["g_ready"], 1)
                    exp_scores(0, v)
                elif step == 1:
                    act.wait_ge(E["rz_ready"], v)
                    A_(zf[:], rx[:], ACT.Ln, scale=lbc[:, 5, ds(v - 1, 1)], bias=lbc[:, 4, ds(v - 1, 1)]).then_inc(E["lf_ready"], 1)
                    exp_scores(1, v)
                    act.wait_ge(E["key_ready"], v)
                    act.wait_ge(E["q_ready"], v)
                    A_(ex[:], qh[:], ACT.Exp, scale=-1.0).then_inc(E["eq_ready"], 1)
                elif step == 2:
                    act.wait_ge(E["cum_ready"], v)
                    A_(eb[:], cum[:], ACT.Exp).then_inc(E["eb_ready"], 1)
                    factor(0, v)
                elif step == 3:
                    act.wait_ge(E["rq_ready"], v)
                    act.wait_ge(E["g_ready"], v)
                    A_(ex[:], gh[:], ACT.Exp, scale=-1.0).then_inc(E["eg_ready"], 1)
                    factor(1, v)
                elif step == 4:
                    take_pv(1, v)
                    act.wait_ge(E["kdT_done"], v)
                    act.copy(kdn[:].rearrange("p a b -> p (a b)"), TA[:]).then_inc(E["kdn_ready"], 1)
                    factor(2, v)
                elif step == 5:
                    factor(3, v)
                    factor(4, v)
                elif step == 6:
                    factor(5, v)
                    factor(6, v)
                elif step == 9:
                    act.wait_ge(E["oT_done"], v)
                    act.wait_ge(xl_ready, level(v, 5, 6))
                    A_(dif[:, 1, :], PB[:], ACT.Square).then_inc(E["sq_ready"], 1)
                elif step == HEAD_PIECES:
                    act.wait_ge(E["ss_done"], v)
                    act.wait_ge(E["gs_ready"], v)
                    A_(rx[:], TB[:], ACT.Ln, scale=1.0 / P, bias=eps_c).then_inc(E["o_ln"], 1)
                    act.wait_ge(E["o_ln"], v)
                    A_(rx[:], rx[:], ACT.Exp, scale=-0.5).then_inc(E["r_ready"], 1)

            def fetch_k(h):
                for e in range(2):
                    act.dma_start(kcur[CHUNK * e:CHUNK * (e + 1), e, :], k_scr[ds(h, 1)].rearrange("a d t -> (a d) t")
                                  ).then_inc(E["kcur_landed"], 16)

            def fetch_v(h):
                for e in range(2):
                    act.dma_start(vcur[:, :, CHUNK * e:CHUNK * (e + 1)],
                                  v_scr[ds(h, 1)].rearrange("a i p d -> p (a i) d")).then_inc(E["vcur_landed"], 16)

            def take_block(k, h, base, it):
                done = base + it * (2 * HEAD_PIECES)
                if k == 2:
                    act.wait_ge(multiplied, done + 2)
                    act.wait_ge(E["scores"], both(h, 1))
                    act.copy(qa[:], A[0][:]).then_inc(E["qa_ready"], 1)
                    if isinstance(h, int) and h == 0:
                        act.wait_ge(kv_stored, 16 * 16)
                        act.wait_ge(temps_ready, 1)
                        fetch_v(h)
                    fetch_k(h)
                elif k == 4:
                    act.wait_ge(multiplied, done + 4)
                    act.wait_ge(E["vT_done"], h)
                    act.copy(iraw[:], A[1][:]).then_inc(E["i_ready"], 1)
                    if not (isinstance(h, int) and h == 0):
                        act.wait_ge(E["pv"], both(h, 1))
                        fetch_v(h)
                elif k == 7:
                    act.wait_ge(multiplied, done + 6)
                    act.wait_ge(E["diag_done"], h)
                    act.wait_ge(xl_ready, level(h, 6, 6))
                    act.wait_ge(E["qb_ready"], h)
                    act.copy(qh[:], A[2][:]).then_inc(E["q_ready"], 1)

            def head_step(h, base, nbase, it, mixing, first=False):
                gp = 2 * HEAD_PIECES
                split_hi(act, base, nbase, it, gp if mixing else 0, gp)
                for k in range(HEAD_PIECES):
                    if mixing and k in (2, 3):
                        attention_first(k, h)
                    if k + 1 < HEAD_PIECES:
                        split_hi(act, base + k + 1, nbase + k + 1, it, gp, gp)
                    if mixing:
                        if k == 0:
                            if not first:
                                mix(HEAD_PIECES, h - 1)
                            act.wait_ge(multiplied, base + it * gp)
                        mix(k, h)
                    take_block(k, h, base, it)

            head_step(0, P1, N1, 0, False)
            head_step(1, P1 + HEAD_PIECES, N1 + HEAD_PIECES, 0, True, first=True)
            with act.Fori(0, 3) as it:
                for r in range(2):
                    head_step(it * 2 + (2 + r), P1 + (2 + r) * HEAD_PIECES, N1 + (2 + r) * HEAD_PIECES, it, True)

            def pair(it, peeled):
                per = len(PAIR)
                split_hi(act, P2, N2, it, PAIR_PIECES, per)
                if peeled:
                    act.wait_ge(multiplied, P2)
                for k in range(PAIR_PIECES):
                    if peeled and k in (2, 3):
                        attention_first(k, HEADS)
                    if k + 1 < PAIR_PIECES:
                        split_hi(act, P2 + k + 1, N2 + PAIR_POS[("w", k + 1)], it, PAIR_PIECES, per)
                    if peeled and k == 0:
                        mix(HEAD_PIECES, HEADS - 1)
                    if peeled and k < HEAD_PIECES:
                        mix(k, HEADS)
                        if k == HEAD_PIECES - 1:
                            mix(HEAD_PIECES, HEADS)
                    if peeled and k in (5, 6):
                        act.wait_ge(E["pv_out"], both(HEADS, 1))
                        for j in range((k - 5) * HEADS // 2, (k - 4) * HEADS // 2):
                            act.copy(o_hi[:, j, :], o_raw[:, j, :]).then_inc(o_hi_ready, 1)
                    if peeled and k == HEAD_PIECES - 1:
                        for j in range(HEADS, 2 * HEADS):
                            act.wait_ge(E["o_ready"], HEADS)
                            act.copy(o_hi[:, j, :], o_raw[:, j, :]).then_inc(o_hi_ready, 1)
                    if k in (2, 4, 6, 7):
                        q = (2, 4, 6, 7).index(k)
                        act.wait_ge(multiplied, P2 + (2, 4, 6, 8)[q] + it * PAIR_PIECES)
                        bank = (A[0], A[1], A[2], A[0])[q]
                        if not peeled:
                            act.wait_ge(merged_ready, 2 * it - 1 + q % 2)
                        A_(small[:, q, :], bank[:], ACT.Sigmoid).then_inc(gate_ready, 1)

            pair(0, True)
            with act.Fori(1, KT // 2) as it:
                pair(it, False)

            split_hi(act, P3, N3)
            for kb in range(KT):
                if kb == 2:
                    split_hi(act, P3 + 1, N3 + 1)
                act.wait_ge(merged_ready, kb + 1)
                act.wait_ge(multiplied, P3)
                act.copy(m_hi[:, kb, :], merged[:, kb, :]).then_inc(mh_ready, 1)
            act.wait_ge(gcol_turned, 1)
            act.copy(small[0:2 * KT, 0, 0:P], SC1[0:2 * KT, 0:P]).then_inc(grow_ready, 1)

            def squares(cg):
                act.wait_ge(multiplied, P3 + 8 * cg + 8)
                for t4 in range(TT):
                    act.wait_ge(y1_sq, 4 * cg + t4)
                    A_(acc[:], OUT_BANKS[cg % 2][t4], ACT.Square,
                       accum_out=ssg[:, 4 * cg + t4:4 * cg + t4 + 1]).then_inc(y1_sq, 1)
            for i in range(2, 32):
                split_hi(act, P3 + i, N3 + i)
                if i % 8 == 1:
                    squares(i // 8 - 1)
            squares(3)

            act.wait_ge(y_sum, 1)
            A_(rms, ssq, ACT.Sqrt, scale=1.0 / D, bias=eps_c).then_inc(root_ready, 1)
            for i in range(TT):
                act.wait_ge(x2_ready, i + 1)
                A_(x2_junk[:], y1[:, i, :], ACT.Square, accum_out=ssq2[:, i:i + 1]).then_inc(x2_sq, 1)
                act.wait_ge(x2_sq, i + 1)
                A_(rms2[:, i:i + 1], ssq2[:, i:i + 1], ACT.Sqrt, scale=1.0 / D, bias=eps_c).then_inc(x2_root, 1)
            split_hi(act, P4, N4)
            split_hi(act, P4 + 1, N4 + 1)
            for kb in range(KT):
                act.wait_ge(h2_turned, kb + 1)
                if kb >= 4:
                    act.wait_ge(h2_ready, kb - 3)
                A_(small[:, kb % 4, :], TURN4[kb % 4], ACT.Identity, scale=a1[:, 1, kb:kb + 1],
                   bias=modc[:, MOD_SH2 + kb:MOD_SH2 + kb + 1]).then_inc(h2x, 1)

            def up(it, peeled):
                for k in range(4):
                    if not (peeled and k < 2):
                        split_hi(act, P4 + k, N4 + k, it, 4, 4)
                    if k == 1 and not peeled:
                        gelu(it)
            def gelu(it):
                act.wait_ge(conv_step, it * 3)
                A_(small[:, 1, :], small[:, 0, :], ACT.Gelu_apprx_tanh).then_inc(gelu_ready, 1)
            up(0, True)
            with act.Fori(1, FB) as it:
                up(it, False)
            gelu(FB)

            def down(u, it=0):
                split_hi(act, P5 + u, N5 + u, it, 4, 4)
                kt = u % FB
                src = act_t[:, ds(it * 4 + kt, 1), :].rearrange("p a b -> p (a b)") if not isinstance(it, int) else act_t[:, kt, :]
                act.copy(a_hi[:, u % 2, :], src).then_inc(ah_ready, 1)

            def y_rms(i):
                act.wait_ge(y_sum, i + 2)
                A_(rms[:, i:i + 1], ssq[:, i:i + 1], ACT.Sqrt, scale=1.0 / D, bias=eps_c).then_inc(y_root, 1)

            for s in range(2):
                base = s * FB
                for u in range(3):
                    if s == 0:
                        act.wait_ge(act_ready, FB - 1 if u < 2 else FB)
                    down(base + u)
                    if u == 0 and s == 1:
                        sweep_out_act(act, 0)
                with act.Fori(0, 10) as it:
                    for i in range(4):
                        down(base + 3 + i, it)
            for i in range(TT):
                sweep_out_act(act, 1, (2 * i, 2 * i + 1))
                if i:
                    y_rms(i - 1)
            y_rms(TT - 1)

        @block.vector
        def _(dve):
            chain = [0]

            def link(ins):
                chain[0] += 1
                ins.then_inc(setup_dve, 1)
                dve.wait_ge(setup_dve, chain[0])

            TTe, TS, STT = dve.tensor_tensor, dve.tensor_scalar, dve.scalar_tensor_tensor
            for h in range(2 * HEADS):
                dve.memset(slope[:, h:h + 1], -(2.0 ** (-8.0 * (h + 1) / (2 * HEADS))))
            dve.wait_ge(vec_turned, 1)
            for j, rows in enumerate((P, 72 + FB, 2 * FB, FB)):
                t = dve.tensor_copy(vec[:, j, 0:rows], SC1[:, j * P:j * P + rows])
            t.then_inc(vec_ready, 1)
            dve.wait_ge(vec_ready, 1)
            l0, l1 = bound_c[:, 0:8], bound_c[:, 8:16]
            link(TTe(lbc[:, 2, :], l0, l1, ALU.max))
            TTe(lbc[:, 0, :], l0, lbc[:, 2, :], ALU.subtract)
            TTe(lbc[:, 1, :], l1, lbc[:, 2, :], ALU.subtract).then_inc(bounds_in, 1)
            dve.wait_ge(c_exp, 1)
            link(TS(csil[:], csil[:], 1.0, None, ALU.add))
            link(dve.reciprocal(csil[:], csil[:]))
            link(TTe(csil[:], csil[:], c_c, ALU.mult))
            dve.wait_ge(bounds_exp, 1)
            link(TTe(lbc[:, 3, :], lbc[:, 2, :], lbc[:, 3, :], ALU.add))
            link(dve.reciprocal(lbc[:, 3, :], lbc[:, 3, :]))
            link(TTe(lbc[:, 4, :], lbc[:, 2, :], lbc[:, 3, :], ALU.mult))
            TS(lbc[:, 5, :], lbc[:, 4, :], -1.0, 1.0, ALU.mult, ALU.add).then_inc(bounds_ready, 1)
            def mod_half(dst, op_no, n, half, kt, it=0, per=0, rawper=0, ktstep=0, static_kt=True):
                if half == 0:
                    dve.wait_ge(landed[n % RAW], 16 * (n // RAW + 1) + it * (16 * (rawper // RAW)))
                w = piece(raw[n % RAW], 2)[:, half, :]
                cs = csil[:, kt:kt + 1] if static_kt else csil[:, ds(it * ktstep + kt, 1)]
                if isinstance(dst, list):
                    if kt < 2 and static_kt:
                        return TS(dst[half], w, cs, None, ALU.mult).then_inc(mod_ops, 1)
                    dve.wait_ge(mod_ops, op_no - 1 + it * per)
                    return STT(dst[half], w, cs, dst[half], ALU.mult, ALU.add).then_inc(mod_ops, 1)
                if kt == 0 and static_kt:
                    return TS(dst, w, cs, None, ALU.mult).then_inc(mod_ops, 1)
                dve.wait_ge(mod_ops, op_no + it * per)
                return STT(dst, w, cs, dst, ALU.mult, ALU.add).then_inc(mod_ops, 1)

            def take_cols(first, count_before, it=0, ip=0, dyn=0):
                dve.wait_ge(mod_summed, count_before + 1 + it * ip)
                if dyn:
                    o, b = modc[:, ds(it * dyn + first, 4)], bmod_c[:, ds(it * dyn + first, 4)]
                else:
                    o, b = modc[:, first:first + 4], bmod_c[:, first:first + 4]
                return TTe(o, mod_bank(count_before)[:, 0:4], b, ALU.add).then_inc(mod_taken, 1)

            def h_low(kb):
                dve.wait_ge(hh_ready, kb + 1)
                TTe(h_lo[:, kb, :], small[:, 2 + kb % 2, :], h_hi[:, kb, :].bitcast(F32), ALU.subtract).then_inc(h_ready, 1)

            def columns(ch):
                take_cols(MOD_SC1 + 4 * ch, 2 * ch)
                take_cols(MOD_SH1 + 4 * ch, 2 * ch + 1)
                dve.wait_ge(mod_taken, 2 * ch + 2)
                STT(a1[:, 0, 4 * ch:4 * ch + 4], modc[:, MOD_SC1 + 4 * ch:MOD_SC1 + 4 * ch + 4], 1.0,
                    pre_mix_c[:, 4 * ch:4 * ch + 4], ALU.add, ALU.mult).then_inc(cols_ready, 1)

            for i in range(8):
                for half in range(2):
                    mod_half(SC1_SUMS, 2 * i + half, i, half, 2 * i + half)
            dve.wait_ge(root_ready, 1)
            dve.reciprocal(rms, rms).then_inc(rms_ready, 1)
            for dst in SH1_SUMS:
                link(dve.memset(dst, 0.0))
            with dve.Fori(0, 2) as it:
                for i in range(4):
                    for half in range(2):
                        mod_half(SH1_SUMS, 2 * (8 + i) + half, 8 + i, half, 2 * i + half, it, 8, 4, 8, False)
            n, m = 16, 16
            for ch in range(1, 4):
                dve.wait_ge(mod_summed, 2 * ch - 1)
                for i in range(8):
                    for half in range(2):
                        mod_half(SC1_SUMS, 2 * (m + i) + half, n + i, half, 2 * i + half)
                    if i == 2:
                        columns(ch - 1)
                    if i >= 4:
                        h_low(4 * (ch - 1) + i - 4)
                split_lo(dve, 2 * ch - 2, kv_pos(2 * ch - 2))
                n, m = n + 9, m + 8
                for dst in SH1_SUMS:
                    link(dve.memset(dst, 0.0))
                with dve.Fori(0, 2) as it:
                    for i in range(4):
                        for half in range(2):
                            mod_half(SH1_SUMS, 2 * (m + i) + half, n + i, half, 2 * i + half, it, 8, 4, 8, False)
                n, m = n + 9, m + 8
                split_lo(dve, 2 * ch - 1, kv_pos(2 * ch - 1))
            columns(3)
            for kb in range(12, 16):
                h_low(kb)
            for g in (KV_PIECES - 2, KV_PIECES - 1):
                split_lo(dve, g, kv_pos(g))


            class Order:
                def __init__(self, v):
                    self.v, self.n = v, 0

                def link(self, ins):
                    self.n += 1
                    ins.then_inc(d_order, 1)
                    dve.wait_ge(d_order, self.v * ORD - (ORD - self.n))

            def soften(e, v, order):
                order.link(STT(bias_t[:], dist[:], slope[:, ds(v * 2 + (e - 2), 1)], band[:], ALU.mult, ALU.add))
                dve.wait_ge(E["scores"], both(v, e))
                dve.wait_ge(E["pT"], both(v - 1, 1))
                sc = SC[:].rearrange("p (i w) -> p i w", w=256)
                STT(prob[:, e, 1:4, CHUNK:256], sc[:, 1:4, CHUNK:256], 0.125,
                    bias_t[:].unsqueeze(1).to_broadcast([P, 3, 192]), ALU.mult, ALU.add)
                STT(prob[:, e, 0, P:256], sc[:, 0, P:256], 0.125, bias_t[:, CHUNK:192], ALU.mult, ALU.add
                    ).then_inc(E["s_taken"], 1)
                dve.wait_ge(E["s_taken"], both(v, e))
                dve.tensor_reduce(smx[e][:, 1:4], prob[:, e, 1:4, CHUNK:256], AX.X, ALU.max)
                order.link(dve.tensor_reduce(smx[e][:, 0:1], prob[:, e, 0, P:256], AX.X, ALU.max))
                TS(smx[e], smx[e], sink[:, ds(v * 2 + (e - 2), 1)], -1.0, ALU.max, ALU.mult).then_inc(E["negmax"], 1)

            def normalise(e, v, order):
                dve.wait_ge(E["p_exp"], both(v, e))
                order.link(TTe(den[e], den[e], esk[e], ALU.add))
                order.link(dve.reciprocal(den[e], den[e]))
                TTe(prob[:, e, :, CHUNK:256], prob[:, e, :, CHUNK:256],
                    den[e].unsqueeze(2).to_broadcast([P, TT, 192]), ALU.mult).then_inc(E["prob"], 1)

            def take_own(e, v):
                dve.wait_ge(E["pT"], both(v, e))
                if e == 1:
                    dve.wait_ge(E["pv"], both(v, 0))
                else:
                    dve.wait_ge(E["pv"], both(v - 1, 1))
                dve.tensor_copy(probT[:, 0, :, :].rearrange("p a b -> p (a b)"), TA[:]).then_inc(E["pT_own"], 1)

            def gate(src_sem, done_sem, v):
                dve.wait_ge(E[src_sem], v)
                return TS(rx[:], ex[:], 1.0, None, ALU.add)

            def diff(u, v):
                slot = dif[:, u % 2, :]
                if u == 0:
                    dve.wait_ge(E["o_ready"], v - 1)
                    c3, d3 = cum[:].rearrange("p (n q) -> p n q", q=CHUNK), slot.rearrange("p (n q) -> p n q", q=CHUNK)
                    return TTe(d3, c3[:, :, CHUNK - 1:CHUNK].to_broadcast([P, NCH, CHUNK]), c3, ALU.subtract
                               ).then_inc(dif_ready, 1)
                if u == 2:
                    dve.wait_ge(E["kdT_done"], v)
                if u >= 3:
                    dve.wait_ge(xl_ready, level(v, u - 2, 6))
                m = LEVELS[u - 1]
                cv, dv = level_view(cum[:], m), level_view(slot, m)
                ref = cv[:, :, 0, m - 1:m].to_broadcast([P, T // (2 * m), m])
                TTe(dv[:, :, 0, :], ref, cv[:, :, 0, :], ALU.subtract)
                TTe(dv[:, :, 1, :], cv[:, :, 1, :], ref, ALU.subtract).then_inc(dif_ready, 1)

            def factors(u, v):
                dve.wait_ge(fac_ready, level(v, u, 7))
                if u >= 3:
                    dve.wait_ge(lev_done, level(v, u - 2, 6))
                m = LEVELS[u - 1]
                xv, dv = level_view(xlev[:, u % 2, :], m), level_view(dif[:, u % 2, :], m)
                kv, qv = level_view(key[:], m), level_view(qh[:], m)
                TTe(xv[:, :, 0, :], kv[:, :, 0, :], dv[:, :, 0, :], ALU.mult)
                TTe(xv[:, :, 1, :], qv[:, :, 1, :], dv[:, :, 1, :], ALU.mult).then_inc(xl_ready, 1)

            def absorb(u, v):
                dve.wait_ge(lev_done, level(v, u, 6))
                m = LEVELS[u - 1]
                bank = (TA, TB)[u % 2]
                sv = level_view(S[:], m)[:, :, 1, :]
                gtmp = gtmps[u % 2]
                own = gtmp.rearrange("p (n m) -> p n m", m=m)
                TTe(gtmp.rearrange("p (i c) -> p i c", c=CHUNK), bank[:, 0:T // 2].rearrange("p (i c) -> p i c", c=CHUNK),
                    lev_mask[:, u - 1, :].unsqueeze(1).to_broadcast([P, TT, CHUNK]), ALU.mult).then_inc(lev_masked, 1)
                dve.wait_ge(lev_masked, level(v, u, 6))
                if u > 1:
                    dve.wait_ge(lev_kept, level(v, u - 1, 6))
                TTe(sv, sv, own, ALU.add).then_inc(lev_kept, 1)

            def finish(v):
                dve.wait_ge(E["r_ready"], v)
                dve.wait_ge(E["gs_ready"], v)
                TTe(dif[:, 0, :], PB[:], rx[:], ALU.mult).then_inc(E["o_scaled"], 1)
                dve.wait_ge(E["o_scaled"], v)
                TTe(o_raw[:, ds(v + (HEADS - 1), 1), :].rearrange("p a b -> p (a b)"), dif[:, 0, :], gh[:], ALU.mult
                    ).then_inc(E["o_ready"], 1)

            def attention_first(k, v, order):
                if k == 2:
                    take_own(0, v)
                    normalise(1, v, order)
                else:
                    take_own(1, v)

            def mix(step, v, order, first=False):
                if step == 0:
                    soften(0, v, order)
                    if not first:
                        finish(v - 1)
                    order.link(gate("ez_ready", None, v))
                    dve.reciprocal(rx[:], rx[:]).then_inc(E["rz_ready"], 1)
                elif step == 1:
                    normalise(0, v, order)
                    dve.wait_ge(E["rz_ready"], v)
                    STT(key[:], ex[:], lbc[:, 5, ds(v - 1, 1)], rx[:], ALU.mult, ALU.mult).then_inc(E["key_ready"], 1)
                    soften(1, v, order)
                    dve.wait_ge(E["lf_ready"], v)
                    dve.tensor_tensor_scan(cum[:], keep[:], zf[:], 0.0, ALU.mult, ALU.add).then_inc(E["cum_ready"], 1)
                elif step == 2:
                    dve.wait_ge(E["cum_ready"], v)
                    diff(0, v)
                    order.link(gate("eq_ready", None, v))
                    order.link(dve.reciprocal(rx[:], rx[:]))
                    TTe(qh[:], qh[:], rx[:], ALU.mult).then_inc(E["rq_ready"], 1)
                elif step == 3:
                    dve.wait_ge(fac_ready, level(v, 0, 7))
                    dve.wait_ge(E["key_ready"], v)
                    TTe(dif[:, 0, :], key[:], dif[:, 0, :], ALU.mult).then_inc(E["kd_ready"], 1)
                    diff(1, v)
                    dve.wait_ge(E["eb_ready"], v)
                    dve.wait_ge(E["rq_ready"], v)
                    dve.wait_ge(E["oT_done"], v - 1)
                    TTe(qb[:], qh[:], eb[:], ALU.mult).then_inc(E["qb_ready"], 1)
                elif step == 4:
                    factors(1, v)
                    diff(2, v)
                elif step == 5:
                    factors(2, v)
                    diff(3, v)
                    diff(4, v)
                    dve.wait_ge(E["diag_done"], v)
                    dve.wait_ge(E["oT_done"], v - 1)
                    TTe(S[:].rearrange("p (i t) -> p i t", t=P), TB[:].rearrange("p (i t) -> p i t", t=P),
                        ident[:].unsqueeze(1).to_broadcast([P, TT, P]), ALU.mult).then_inc(E["S_ready"], 1)
                    dve.wait_ge(E["U_done"], v)
                    order.link(dve.tensor_copy(state[:, 1, :], chunk_sum(0)))
                    for ch in range(1, NCH - 1):
                        t = STT(state[:, ch + 1, :], state[:, ch, :], eb[:, CHUNK * ch + CHUNK - 1:CHUNK * (ch + 1)],
                                chunk_sum(ch), ALU.mult, ALU.add)
                        if ch < NCH - 2:
                            t.then_inc(E["o_part"], 1)
                            dve.wait_ge(E["o_part"], v * 5 - (5 - ch))
                    order.link(t)
                elif step == 6:
                    dve.wait_ge(E["S_ready"], v)
                    absorb(1, v)
                    factors(3, v)
                    absorb(2, v)
                    factors(4, v)
                    diff(5, v)
                    diff(6, v)
                elif step == 7:
                    absorb(3, v)
                    factors(5, v)
                    absorb(4, v)
                    factors(6, v)
                elif step == 8:
                    absorb(5, v)
                    absorb(6, v)
                    order.link(gate("eg_ready", None, v))
                    order.link(dve.reciprocal(rx[:], rx[:]))
                    STT(gh[:], gh[:], hgn_c[:, ds(v - 1, 1)], rx[:], ALU.mult, ALU.mult).then_inc(E["gs_ready"], 1)
                    assert order.n == ORD, order.n

            def head_step(h, base, nbase, it, mixing, first=False):
                order = Order(h)
                gp = 2 * HEAD_PIECES
                split_lo(dve, base, nbase, it, gp)
                for k in range(HEAD_PIECES):
                    if mixing and k in (2, 3):
                        attention_first(k, h, order)
                    if k + 1 < HEAD_PIECES:
                        split_lo(dve, base + k + 1, nbase + k + 1, it, gp)
                    if mixing:
                        mix(k, h, order, first)
                    if k == 8:
                        dve.wait_ge(multiplied, base + 8 + it * gp)
                        TS(zf[:], A[0][:], -69.0, None, ALU.max).then_inc(E["z_ready"], 1)

            head_step(0, P1, N1, 0, False)
            dve.wait_ge(kv_stored, 16 * 16)
            dve.wait_ge(temps_ready, 1)
            dve.wait_ge(bounds_ready, 1)
            head_step(1, P1 + HEAD_PIECES, N1 + HEAD_PIECES, 0, True, first=True)
            with dve.Fori(0, 3) as it:
                for r in range(2):
                    head_step(it * 2 + (2 + r), P1 + (2 + r) * HEAD_PIECES, N1 + (2 + r) * HEAD_PIECES, it, True)

            def pair(it, peeled):
                per = len(PAIR)
                order = Order(HEADS)
                split_lo(dve, P2, N2, it, PAIR_PIECES)
                m = 0
                for k in range(PAIR_PIECES):
                    if peeled and k in (2, 3):
                        attention_first(k, HEADS, order)
                    if k + 1 < PAIR_PIECES:
                        split_lo(dve, P2 + k + 1, N2 + PAIR_POS[("w", k + 1)], it, PAIR_PIECES)
                    if k == 0 and not peeled:
                        weighed(3, it - 1)
                        merge(1, it - 1)
                    if peeled and k < HEAD_PIECES:
                        mix(k, HEADS, order)
                    if peeled and k == 7:
                        o_low(0)
                    if peeled and k == HEAD_PIECES - 1:
                        finish(HEADS)
                        o_low(HEADS)
                    for _ in range(MODS_IN_STEP[k]):
                        pc, kk = divmod(m, 8)
                        if kk == 0:
                            dve.wait_ge(mod_summed, 8 + pc + 2 * it)
                        for half in range(2):
                            mod_half(acc[:], 2 * (MODS_HEAD + m) + half, N2 + PAIR_POS[("m", m)], half, 2 * kk + half,
                                     it, 2 * PAIR_MODS, per)
                        if kk == 7 and pc == 0:
                            take_cols(MOD_G1, 8, it, 2, 0 if isinstance(it, int) else 8)
                        m += 1
                    if k == 9:
                        weighed(0, it)
                    if k == 10:
                        weighed(1, it)
                    if k == 11:
                        take_cols(MOD_G1 + 4, 9, it, 2, 0 if isinstance(it, int) else 8)
                        weighed(2, it)
                        merge(0, it)

            def o_low(j0):
                for j in range(j0, j0 + HEADS):
                    dve.wait_ge(o_hi_ready, j + 1)
                    TTe(o_lo[:, j, :], o_raw[:, j, :], o_hi[:, j, :].bitcast(F32), ALU.subtract).then_inc(o_split, 1)

            def weighed(q, it):
                dve.wait_ge(multiplied, P2 + 9 + q + it * PAIR_PIECES)
                dve.wait_ge(gate_ready, q + 1 + 4 * it)
                TTe(small[:, q, :], small[:, q, :], (A[1], A[2], A[0], A[1])[q][:], ALU.mult).then_inc(ga_used, 1)

            def merge(j, it):
                dve.wait_ge(ga_used, 4 * it + j + 3)
                TTe(merged[:, ds(it * 2 + j, 1), :].rearrange("p a b -> p (a b)"), small[:, j, :], small[:, j + 2, :],
                    ALU.add).then_inc(merged_ready, 1)

            pair(0, True)
            with dve.Fori(1, KT // 2) as it:
                pair(it, False)
            weighed(3, KT // 2 - 1)
            merge(1, KT // 2 - 1)
            dve.wait_ge(mod_taken, 24)
            TTe(gcol[:, 0, :], modc[:, MOD_G1:MOD_G1 + KT], post_mix_c, ALU.mult)
            STT(a1[:, 1, :], modc[:, MOD_SC2:MOD_SC2 + KT], 1.0, pre_ffn_c, ALU.add, ALU.mult).then_inc(y1_out, 1)
            TTe(gcol[:, 1, :], modc[:, MOD_G2:MOD_G2 + KT], post_ffn_c, ALU.mult).then_inc(gcol_ready, 1)

            split_lo(dve, P3, N3)
            for kb in range(KT):
                if kb == 2:
                    split_lo(dve, P3 + 1, N3 + 1)
                dve.wait_ge(mh_ready, kb + 1)
                TTe(m_lo[:, kb, :], merged[:, kb, :], m_hi[:, kb, :].bitcast(F32), ALU.subtract).then_inc(m_split, 1)
            def products(cg):
                if cg == 0:
                    dve.wait_ge(gain1_landed, 16)
                dve.wait_ge(multiplied, P3 + 8 * cg + 8)
                for t4 in range(TT):
                    dve.wait_ge(y1_sq, 4 * cg + t4 + 1)
                    TTe(y1[:, t4, cg * 512:(cg + 1) * 512], OUT_BANKS[cg % 2][t4], gain1[:, cg * 512:(cg + 1) * 512],
                        ALU.mult).then_inc(y1_out, 1)
            for i in range(2, 32):
                split_lo(dve, P3 + i, N3 + i)
                if i % 8 == 1:
                    products(i // 8 - 1)
            products(3)
            dve.wait_ge(y1_sq, 16)
            dve.tensor_reduce(ssq, ssg.rearrange("p (g t) -> p t g", t=4), AX.X, ALU.add).then_inc(y_sum, 1)
            dve.wait_ge(root_ready, 2)
            link(dve.reciprocal(rms, rms))
            dve.wait_ge(x3_landed, 64)
            dve.wait_ge(y1_out, 17)
            for i in range(TT):
                STT(y1[:, i, :], y1[:, i, :], rms[:, i:i + 1], x_again[:, i, :], ALU.mult, ALU.add).then_inc(x2_ready, 1)
            for i in range(TT):
                dve.wait_ge(x2_root, i + 1)
                dve.reciprocal(rms2[:, i:i + 1], rms2[:, i:i + 1]).then_inc(x2_rms, 1)
                dve.wait_ge(x2_rms, i + 1)
                TS(diag[:, i, :], ident[:], rms2[:, i:i + 1], None, ALU.mult).then_inc(diag_ready, 1)
            split_lo(dve, P4, N4)
            split_lo(dve, P4 + 1, N4 + 1)
            for kb in range(KT + 1):
                if kb < KT:
                    dve.wait_ge(h2x, kb + 1)
                    dve.tensor_copy(h_hi[:, kb, :], small[:, kb % 4, :]).then_inc(h2h, 1)
                if kb:
                    j = kb - 1
                    dve.wait_ge(h2h, j + 1)
                    TTe(h_lo[:, j, :], small[:, j % 4, :], h_hi[:, j, :].bitcast(F32), ALU.subtract).then_inc(h2_ready, 1)

            def up(it, peeled):
                for k in range(4):
                    if not (peeled and k < 2):
                        split_lo(dve, P4 + k, N4 + k, it, 4)
                    if k == 1 and not peeled:
                        weigh(it)
                    if k == 3:
                        conv(it)

            def conv(it):
                j = (lambda v: v[:, 0:1]) if isinstance(it, int) else (lambda v: v[:, ds(it, 1)])
                dve.wait_ge(multiplied, P4 + 2 + it * 4)
                cv, a = small[:, 0, :], A[0]
                dve.wait_ge(gelu_ready, it)
                TS(cv, a[:], j(tap_c[2]), j(convb_c), ALU.mult, ALU.add).then_inc(conv_step, 1)
                dve.wait_ge(conv_step, 3 * it + 1)
                STT(cv[:, 1:T], a[:, 0:T - 1], j(tap_c[1]), cv[:, 1:T], ALU.mult, ALU.add).then_inc(conv_step, 1)
                dve.wait_ge(conv_step, 3 * it + 2)
                STT(cv[:, 2:T], a[:, 0:T - 2], j(tap_c[0]), cv[:, 2:T], ALU.mult, ALU.add).then_inc(conv_step, 1)

            def weigh(it):
                dve.wait_ge(gelu_ready, it)
                dve.wait_ge(multiplied, P4 + it * 4)
                dst = act_t[:, ds(it - 1, 1), :].rearrange("p a b -> p (a b)") if not isinstance(it, int) else act_t[:, it - 1, :]
                TTe(dst, small[:, 1, :], A[1][:], ALU.mult).then_inc(act_ready, 1)

            up(0, True)
            dve.wait_ge(x2_stored, 64)
            with dve.Fori(1, FB) as it:
                up(it, False)
            weigh(FB)
            dve.wait_ge(act_ready, FB)

            def down(u, it=0):
                split_lo(dve, P5 + u, N5 + u, it, 4)
                kt = u % FB
                dve.wait_ge(ah_ready, u + 1 + it * 4)
                src = act_t[:, ds(it * 4 + kt, 1), :].rearrange("p a b -> p (a b)") if not isinstance(it, int) else act_t[:, kt, :]
                TTe(a_lo[:, u % 2, :], src, a_hi[:, u % 2, :].bitcast(F32), ALU.subtract).then_inc(al_ready, 1)

            def sweep_out(s, banks=range(8)):
                for b in banks:
                    bank_complete(dve, s, b)
                    c0 = s * 1024 + (b % 2) * 512
                    dve.wait_ge(y2_sq, 8 * s + b + 1)
                    TTe(y2[:, b // 2, c0:c0 + 512], DOWN_BANKS[b], gain2[:, c0:c0 + 512], ALU.mult).then_inc(y2_out, 1)

            for s in range(2):
                base = s * FB
                for u in range(3):
                    down(base + u)
                    if u == 0 and s == 1:
                        dve.wait_ge(gain2_landed, 16)
                        sweep_out(0)
                with dve.Fori(0, 10) as it:
                    for i in range(4):
                        down(base + 3 + i, it)
            for i in range(TT + 1):
                if i < TT:
                    sweep_out(1, (2 * i, 2 * i + 1))
                    dve.wait_ge(y2_sq, 8 + 2 * i + 2)
                    dve.tensor_reduce(ssq[:, i:i + 1], ssg[:, 4 * i:4 * i + 4], AX.X, ALU.add).then_inc(y_sum, 1)
                if i:
                    j = i - 1
                    dve.wait_ge(y_root, i)
                    link(dve.reciprocal(rms[:, j:j + 1], rms[:, j:j + 1]))
                    if j == 0:
                        dve.wait_ge(x2b_landed, 64)
                    dve.wait_ge(y2_out, 8 + 2 * i)
                    STT(y2[:, j, :], y2[:, j, :], rms[:, j:j + 1], x2_again[:, j, :], ALU.mult, ALU.add).then_inc(out_ready, 1)

        @block.gpsimd
        def _(pool):
            cnt = [0]

            def link(ins):
                cnt[0] += 1
                ins.then_inc(pool_order, 1)
                pool.wait_ge(pool_order, cnt[0])

            link(pool.memset(ident[:], 0.0))
            link(pool.affine_select(out=ident[:], in_=ident[:], compare_op=ALU.not_equal, fill=1.0, base=0,
                                    pattern=[[-1, P]], channel_multiplier=1))
            link(pool.memset(ones[:], 1.0))
            pool.memset(st[:, 0:1], EPS).then_inc(consts_ready, 1)

            link(pool.memset(state[:, 0, :], 0.0))
            link(pool.memset(keep[:], 1.0))
            link(pool.memset(keep[:].rearrange("p (n q) -> p n q", q=CHUNK)[:, :, 0:1], 0.0))
            link(pool.memset(lev_mask[:], 1.0))
            for u, m in enumerate(LEVELS):
                nb = CHUNK // m
                lm = lev_mask[:, u, :].rearrange("p (n m) -> p n m", m=m)
                link(pool.affine_select(out=lm, in_=lm, compare_op=ALU.is_ge, fill=0.0, base=0,
                                        pattern=[[-2 * m, nb], [0, m]], channel_multiplier=1))
                link(pool.affine_select(out=lm, in_=lm, compare_op=ALU.is_ge, fill=0.0, base=m - 1,
                                        pattern=[[2 * m, nb], [0, m]], channel_multiplier=-1))
            link(pool.iota(bias_t[:].bitcast(I32), pattern=[[-1, 192]], base=CHUNK, channel_multiplier=1))
            link(pool.tensor_copy(dist[:], bias_t[:].bitcast(I32)))
            link(pool.tensor_scalar(bias_t[:], dist[:], -1.0, 0.0, ALU.mult, ALU.max))
            link(pool.tensor_scalar(dist[:], dist[:], 0.0, None, ALU.max))
            link(pool.tensor_tensor(dist[:], dist[:], bias_t[:], ALU.add))
            link(pool.memset(band[:], 0.0))
            link(pool.memset(band[0:CHUNK, P:192], NEG))
            link(pool.memset(band[CHUNK:P, 0:CHUNK], NEG))

            pool.wait_ge(kv_out, 4)
            for h in range(4):
                lo = CHUNK * (h % 2)
                for r in range(2):
                    pool.dma_start(k_scr[2 * h + r], kvT[lo:lo + CHUNK, h // 2, :]).then_inc(kv_stored, 16)
            link(pool.memset(kcur[:], 0.0))
            pool.memset(prob[:], 0.0).then_inc(temps_ready, 1)
            pool.wait_ge(v_ready, TT)
            v_dst = v_scr.rearrange("(h r) i p d -> p r i h d", r=2)
            for r in range(2):
                for i in range(TT):
                    pool.dma_start(v_dst[:, r, i], v_nat[:, i, :].rearrange("p (h d) -> p h d", h=4)).then_inc(kv_stored, 16)
            pool.wait_ge(kv_stored, 16 * 16)
            pool.wait_ge(multiplied, P3)
            for i in range(TT):
                pool.dma_start(x_again[:, i, :], x_rows[i]).then_inc(x3_landed, 16)
            pool.wait_ge(grow_ready, 1)
            pool.dma_start(g_scr, small[0:2 * KT, 0, 0:P]).then_inc(grow_stored, 16)
            pool.wait_ge(grow_stored, 16)
            row = lambda a: g_scr[a * KT:(a + 1) * KT, :].rearrange("n p -> (n p)").partition_broadcast(P)
            pool.dma_start(gain1[:], row(0)).then_inc(gain1_landed, 16)
            for i in range(TT):
                pool.wait_ge(x2_ready, i + 1)
                pool.dma_start(x2_scr[i], y1[:, i, :]).then_inc(x2_stored, 16)
            pool.wait_ge(h2_turned, KT)
            pool.dma_start(gain2[:], row(1)).then_inc(gain2_landed, 16)
            pool.wait_ge(x2_stored, 64)
            pool.wait_ge(multiplied, P5)
            for i in range(TT):
                pool.dma_start(x2_again[:, i, :], x2_scr[i]).then_inc(x2b_landed, 16)
            pool.wait_ge(x2b_landed, 64)


_INS = ['x', 'c', 'w_mod', 'b_mod', 'pre_mix_norm', 'w_in', 'attn_sinks', 'hg_lower_bounds', 'hg_out_norm',
        'w_branch_a', 'w_branch_b', 'w_out', 'post_mix_norm', 'pre_ffn_norm', 'w_ffn_up', 'ffn_conv_w',
        'ffn_conv_b', 'w_ffn_down', 'post_ffn_norm']


def kernel(**inputs):
    import numpy as np
    import concourse.bacc as bacc
    from concourse.bass_utils import run_bass_kernel_spmd

    nc = bacc.Bacc("TRN2", target_bir_lowering=False, num_devices=1)
    arrays, args = {}, []
    for name in _INS:
        a = np.ascontiguousarray(inputs[name])
        arrays[f"in_{name}_dram"] = a
        args.append(nc.dram_tensor(f"in_{name}_dram", a.shape, mybir.dt.from_np(a.dtype), kind="ExternalInput").ap())
    args.append(nc.dram_tensor("out_0_dram", (1, T, D), F32, kind="ExternalOutput").ap())
    block_kernel(nc, *args)
    r = run_bass_kernel_spmd(nc, [arrays], core_ids=[0])
    return r.results[0]["out_0_dram"]
```
